# Optimizing a Trainium2 kernel written in Bass

```python
import jax
import jax.numpy as jnp
from jax import lax
import numpy as np

D_MODEL = 1024
BATCH = 1
SEQ = 256
DEPTH = 1
DEC_BATCH = 8
DEC_SEQ = 4
PAST_LEN = 256
PAGE_SIZE = 128

HEAD_DIM = 64
N_HEADS_MOBA = D_MODEL // (2 * HEAD_DIM)
N_HEADS_WIN = D_MODEL // (2 * HEAD_DIM)
MOBA_BLOCK = 256
MOBA_TOPK = 3
Q_CHUNK = 128
WIN_PATTERNS = ((128, 1), (512, 4), (2048, 16))
WIN_MAX = 2048
BAND_Q = 128
N_EXPERTS = 32
TOP_K = 4
D_EXPERT = D_MODEL
SWIGLU_LIMIT = 7.0
SWIGLU_ALPHA = 1.702
LN_EPS = 1e-5
RMS_EPS = 1e-6
ATTN_SCALE = HEAD_DIM ** -0.5
DN_ALPHA = (2 * DEPTH) ** 0.25
DN_BETA = (8 * DEPTH) ** -0.25

kernel_name = 'hybrid_moba_longnet_moe_step'

def alibi_slopes(n_heads):
    return jnp.exp2(-8.0 * jnp.arange(1, n_heads + 1, dtype=jnp.float32) / n_heads)

def layer_norm(x, g, b):
    xf = x.astype(jnp.float32)
    mu = jnp.mean(xf, axis=-1, keepdims=True)
    var = jnp.mean(jnp.square(xf - mu), axis=-1, keepdims=True)
    return ((xf - mu) * lax.rsqrt(var + LN_EPS) * g + b).astype(x.dtype)

def head_rmsnorm(o, g):
    of = o.astype(jnp.float32)
    of = of * lax.rsqrt(jnp.mean(jnp.square(of), axis=-1, keepdims=True) + RMS_EPS)
    return of.reshape(of.shape[0], -1) * g

def moba_core(q, qpos, kb, vb, slopes):
    n_blk = kb.shape[0]
    n_q, n_h, _ = q.shape
    qf = q.astype(jnp.float32)
    k_mean = jnp.mean(kb.astype(jnp.float32), axis=1)
    gate = jnp.einsum('qhd,nhd->qhn', qf, k_mean)
    n_cand = max(n_blk, MOBA_TOPK)
    gate = jnp.pad(gate, ((0, 0), (0, 0), (0, n_cand - n_blk)))
    own = qpos // MOBA_BLOCK
    gate = jnp.where(jnp.arange(n_cand)[None, None, :] < own[:, None, None], gate, -jnp.inf)
    _, sel = lax.top_k(gate, MOBA_TOPK)
    sel_ok = jnp.arange(MOBA_TOPK)[None, None, :] < own[:, None, None]
    sel = jnp.where(sel_ok, sel, 0)
    kb_h = jnp.transpose(kb, (2, 0, 1, 3))
    vb_h = jnp.transpose(vb, (2, 0, 1, 3))
    h_idx = jnp.arange(n_h)[None, :, None]
    k_sel = kb_h[h_idx, sel]
    v_sel = vb_h[h_idx, sel]
    k_own = kb[own]
    v_own = vb[own]
    offs = jnp.arange(MOBA_BLOCK)
    dist_sel = (qpos[:, None, None, None] - (sel[..., None] * MOBA_BLOCK + offs)).astype(jnp.float32)
    s_sel = jnp.einsum('qhd,qhcjd->qhcj', qf, k_sel) * ATTN_SCALE - slopes[None, :, None, None] * dist_sel
    s_sel = jnp.where(sel_ok[..., None], s_sel, -jnp.inf).reshape(n_q, n_h, MOBA_TOPK * MOBA_BLOCK)
    dist_own = qpos[:, None] - (own[:, None] * MOBA_BLOCK + offs[None, :])
    s_own = jnp.einsum('qhd,qjhd->qhj', qf, k_own) * ATTN_SCALE - slopes[None, :, None] * dist_own[:, None, :].astype(jnp.float32)
    s_own = jnp.where((dist_own >= 0)[:, None, :], s_own, -jnp.inf)
    p = jax.nn.softmax(jnp.concatenate([s_sel, s_own], axis=-1), axis=-1)
    p_sel = p[..., :MOBA_TOPK * MOBA_BLOCK].reshape(n_q, n_h, MOBA_TOPK, MOBA_BLOCK)
    p_own = p[..., MOBA_TOPK * MOBA_BLOCK:]
    return jnp.einsum('qhcj,qhcjd->qhd', p_sel, v_sel) + jnp.einsum('qhj,qjhd->qhd', p_own, v_own)

def moba_prompt(q, k, v, slopes):
    b, s, h, dh = q.shape
    n_blk = -(-s // MOBA_BLOCK)
    pad = n_blk * MOBA_BLOCK - s
    kb_all = jnp.pad(k, ((0, 0), (0, pad), (0, 0), (0, 0))).reshape(b, n_blk, MOBA_BLOCK, h, dh)
    vb_all = jnp.pad(v, ((0, 0), (0, pad), (0, 0), (0, 0))).reshape(b, n_blk, MOBA_BLOCK, h, dh)
    n_c = s // Q_CHUNK
    q_c = q.reshape(b * n_c, Q_CHUNK, h, dh)
    b_idx = jnp.repeat(jnp.arange(b), n_c)
    q_pos = jnp.tile(jnp.arange(s).reshape(n_c, Q_CHUNK), (b, 1))

    def one(args):
        qq, bi, pos = args
        return moba_core(qq, pos, kb_all[bi], vb_all[bi], slopes)

    return lax.map(one, (q_c, b_idx, q_pos)).reshape(b, s, h, dh)

def moba_sample(q, k, v, cache_k, cache_v, page_table, slopes):
    db, ds, h, dh = q.shape
    past = page_table.shape[1] * cache_k.shape[1]
    total = past + ds
    n_blk = -(-total // MOBA_BLOCK)
    pad = n_blk * MOBA_BLOCK - total
    q_pos = past + jnp.arange(ds)

    def one(args):
        qq, kk, vv, pt = args
        k_seq = jnp.concatenate([cache_k[pt].reshape(past, h, dh), kk], axis=0)
        v_seq = jnp.concatenate([cache_v[pt].reshape(past, h, dh), vv], axis=0)
        k_seq = jnp.pad(k_seq, ((0, pad), (0, 0), (0, 0))).reshape(n_blk, MOBA_BLOCK, h, dh)
        v_seq = jnp.pad(v_seq, ((0, pad), (0, 0), (0, 0))).reshape(n_blk, MOBA_BLOCK, h, dh)
        return moba_core(qq, q_pos, k_seq, v_seq, slopes)

    return lax.map(one, (q, k, v, page_table))

def merge_by_denominator(outs, lses):
    w = jax.nn.softmax(jnp.stack(lses), axis=0)
    return jnp.sum(w[..., None] * jnp.stack(outs), axis=0)

def dilated_prompt(q, k, v, slopes):
    b, s, h, dh = q.shape
    outs, lses = [], []
    for window, dil in WIN_PATTERNS:
        steps = window // dil
        n_sub = s // dil
        n_subp = -(-n_sub // BAND_Q) * BAND_Q
        nb = n_subp // BAND_Q

        def by_residue(a):
            a = jnp.transpose(a.reshape(b, n_sub, dil, h, dh), (0, 2, 1, 3, 4))
            return jnp.pad(a, ((0, 0), (0, 0), (0, n_subp - n_sub), (0, 0), (0, 0)))

        def band(a):
            prev = jnp.pad(a, ((0, 0), (0, 0), (BAND_Q, 0), (0, 0), (0, 0)))[:, :, :n_subp]
            return jnp.concatenate([prev.reshape(b, dil, nb, BAND_Q, h, dh),
                                    a.reshape(b, dil, nb, BAND_Q, h, dh)], axis=3)

        qr = by_residue(q).reshape(b, dil, nb, BAND_Q, h, dh).astype(jnp.float32)
        kband = band(by_residue(k))
        vband = band(by_residue(v))
        sc = jnp.einsum('brnqhd,brnkhd->brnhqk', qr, kband) * ATTN_SCALE
        rel = (BAND_Q + jnp.arange(BAND_Q))[:, None] - jnp.arange(2 * BAND_Q)[None, :]
        k_idx = jnp.arange(nb)[:, None] * BAND_Q + jnp.arange(2 * BAND_Q)[None, :] - BAND_Q
        valid = ((rel >= 0) & (rel <= steps))[None, :, :] & (k_idx >= 0)[:, None, :]
        sc = sc - slopes[:, None, None] * (rel * dil).astype(jnp.float32)
        sc = jnp.where(valid[:, None, :, :], sc, -jnp.inf)
        lse = jax.nn.logsumexp(sc, axis=-1)
        p = jnp.exp(sc - lse[..., None])
        o = jnp.einsum('brnhqk,brnkhd->brnqhd', p, vband).reshape(b, dil, n_subp, h, dh)[:, :, :n_sub]
        outs.append(jnp.transpose(o, (0, 2, 1, 3, 4)).reshape(b, s, h, dh))
        lse = jnp.transpose(lse, (0, 1, 2, 4, 3)).reshape(b, dil, n_subp, h)[:, :, :n_sub]
        lses.append(jnp.transpose(lse, (0, 2, 1, 3)).reshape(b, s, h))
    return merge_by_denominator(outs, lses)

def dilated_sample(q, k, v, k_buf, v_buf, slopes):
    db, ds, h, dh = q.shape
    w_len = k_buf.shape[1]
    kc = jnp.concatenate([k_buf, k], axis=1)
    vc = jnp.concatenate([v_buf, v], axis=1)
    qf = q.astype(jnp.float32)
    outs, lses = [], []
    for window, dil in WIN_PATTERNS:
        j = jnp.arange(window // dil + 1)
        idx = w_len + jnp.arange(ds)[:, None] - j[None, :] * dil
        valid = idx >= 0
        idx = jnp.maximum(idx, 0)
        ks = kc[:, idx]
        vs = vc[:, idx]
        sc = jnp.einsum('bqhd,bqjhd->bhqj', qf, ks) * ATTN_SCALE - slopes[:, None, None] * (j * dil).astype(jnp.float32)[None, None, :]
        sc = jnp.where(valid[None, None], sc, -jnp.inf)
        lse = jax.nn.logsumexp(sc, axis=-1)
        p = jnp.exp(sc - lse[..., None])
        outs.append(jnp.einsum('bhqj,bqjhd->bqhd', p, vs))
        lses.append(jnp.transpose(lse, (0, 2, 1)))
    new_len = min(WIN_MAX, w_len + ds)
    return (merge_by_denominator(outs, lses), kc[:, w_len + ds - new_len:], vc[:, w_len + ds - new_len:])

def moe_ffn(hx, w_router, b_router, w_gate_up, b_gate_up, w_down, b_down):
    m, d = hx.shape
    logits = jnp.matmul(hx, w_router).astype(jnp.float32) + b_router
    top_val, top_idx = lax.top_k(logits, TOP_K)
    gates = jax.nn.softmax(top_val, axis=-1)
    comb = jnp.sum(jax.nn.one_hot(top_idx, N_EXPERTS, dtype=jnp.float32) * gates[..., None], axis=1)

    def expert_step(acc, xs):
        wgu, bgu, wdn, bdn, c = xs
        gu = jnp.matmul(hx, wgu) + bgu
        gate = jnp.minimum(gu[:, 0::2], SWIGLU_LIMIT)
        up = jnp.clip(gu[:, 1::2], -SWIGLU_LIMIT, SWIGLU_LIMIT)
        act = gate * jax.nn.sigmoid(SWIGLU_ALPHA * gate) * (up + 1.0)
        y = jnp.matmul(act, wdn) + bdn
        return acc + c[:, None] * y.astype(jnp.float32), None

    acc, _ = lax.scan(expert_step, jnp.zeros((m, d), jnp.float32),
                      (w_gate_up, b_gate_up, w_down, b_down, comb.T))
    return acc

def trunk_layer(xp, xs, ck, cv, kw, vw, page_table, w_in, gn_moba, gn_win, w_out, ln1_g, ln1_b,
                w_router, b_router, w_gate_up, b_gate_up, w_down, b_down, ln2_g, ln2_b):
    b, s, d = xp.shape
    db, ds, _ = xs.shape
    n_p = b * s
    hd_a = N_HEADS_MOBA * HEAD_DIM
    hd_b = N_HEADS_WIN * HEAD_DIM
    x_all = jnp.concatenate([xp.reshape(n_p, d), xs.reshape(db * ds, d)], axis=0)
    proj = jnp.matmul(x_all, w_in)
    cuts = list(np.cumsum([hd_a, hd_a, hd_a, hd_b, hd_b]))
    qa, ka, va, qb, kb, vb = jnp.split(proj, cuts, axis=-1)

    def heads(t, nh):
        return t[:n_p].reshape(b, s, nh, HEAD_DIM), t[n_p:].reshape(db, ds, nh, HEAD_DIM)

    qa_p, qa_s = heads(qa, N_HEADS_MOBA)
    ka_p, ka_s = heads(ka, N_HEADS_MOBA)
    va_p, va_s = heads(va, N_HEADS_MOBA)
    qb_p, qb_s = heads(qb, N_HEADS_WIN)
    kb_p, kb_s = heads(kb, N_HEADS_WIN)
    vb_p, vb_s = heads(vb, N_HEADS_WIN)
    sl_a = alibi_slopes(N_HEADS_MOBA)
    sl_b = alibi_slopes(N_HEADS_WIN)

    oa_p = moba_prompt(qa_p, ka_p, va_p, sl_a)
    oa_s = moba_sample(qa_s, ka_s, va_s, ck, cv, page_table, sl_a)
    ob_p = dilated_prompt(qb_p, kb_p, vb_p, sl_b)
    ob_s, kw_new, vw_new = dilated_sample(qb_s, kb_s, vb_s, kw, vw, sl_b)

    oa = jnp.concatenate([oa_p.reshape(n_p, N_HEADS_MOBA, HEAD_DIM), oa_s.reshape(db * ds, N_HEADS_MOBA, HEAD_DIM)], axis=0)
    ob = jnp.concatenate([ob_p.reshape(n_p, N_HEADS_WIN, HEAD_DIM), ob_s.reshape(db * ds, N_HEADS_WIN, HEAD_DIM)], axis=0)
    o_cat = jnp.concatenate([head_rmsnorm(oa, gn_moba), head_rmsnorm(ob, gn_win)], axis=-1).astype(x_all.dtype)
    hx = layer_norm(DN_ALPHA * x_all + jnp.matmul(o_cat, w_out), ln1_g, ln1_b)
    f = moe_ffn(hx, w_router, b_router, w_gate_up, b_gate_up, w_down, b_down).astype(hx.dtype)
    hx = layer_norm(DN_ALPHA * hx + f, ln2_g, ln2_b)

    win_p = min(WIN_MAX, s)
    return (hx[:n_p].reshape(b, s, d), hx[n_p:].reshape(db, ds, d),
            ka_p, va_p, ka_s, va_s, kb_p[:, s - win_p:], vb_p[:, s - win_p:], kw_new, vw_new)

def setup_inputs(seed: int = 0) -> dict:
    key = jax.random.key(seed)
    ks = jax.random.split(key, 24)
    f32 = jnp.float32
    n_pages = PAST_LEN // PAGE_SIZE
    n_used = DEC_BATCH * n_pages
    n_pool = n_used + n_used // 4
    wbuf = min(WIN_MAX, PAST_LEN)
    hd_a = N_HEADS_MOBA * HEAD_DIM
    hd_b = N_HEADS_WIN * HEAD_DIM
    mix = hd_a + hd_b
    nrm = jax.random.normal
    x_prompt = nrm(ks[0], (BATCH, SEQ, D_MODEL), f32)
    x_sample = nrm(ks[1], (DEC_BATCH, DEC_SEQ, D_MODEL), f32)
    cache_k_moba = nrm(ks[2], (DEPTH, n_pool, PAGE_SIZE, N_HEADS_MOBA, HEAD_DIM), f32)
    cache_v_moba = DN_BETA * nrm(ks[3], (DEPTH, n_pool, PAGE_SIZE, N_HEADS_MOBA, HEAD_DIM), f32)
    state_k_win = nrm(ks[4], (DEPTH, DEC_BATCH, wbuf, N_HEADS_WIN, HEAD_DIM), f32)
    state_v_win = DN_BETA * nrm(ks[5], (DEPTH, DEC_BATCH, wbuf, N_HEADS_WIN, HEAD_DIM), f32)
    page_table = jax.random.permutation(ks[6], n_pool)[:n_used].reshape(DEC_BATCH, n_pages).astype(jnp.int32)
    col_scale = jnp.concatenate([jnp.ones((2 * hd_a,), f32), jnp.full((hd_a,), DN_BETA, f32),
                                 jnp.ones((2 * hd_b,), f32), jnp.full((hd_b,), DN_BETA, f32)])
    w_in = nrm(ks[7], (DEPTH, D_MODEL, 3 * mix), f32) * (D_MODEL ** -0.5) * col_scale
    gn_moba = 1.0 + 0.02 * nrm(ks[8], (DEPTH, hd_a), f32)
    gn_win = 1.0 + 0.02 * nrm(ks[9], (DEPTH, hd_b), f32)
    w_out = nrm(ks[10], (DEPTH, mix, D_MODEL), f32) * (mix ** -0.5) * DN_BETA
    ln1_g = 1.0 + 0.02 * nrm(ks[11], (DEPTH, D_MODEL), f32)
    ln1_b = 0.02 * nrm(ks[12], (DEPTH, D_MODEL), f32)
    w_router = nrm(ks[13], (DEPTH, D_MODEL, N_EXPERTS), f32) * (D_MODEL ** -0.5)
    b_router = 0.01 * nrm(ks[14], (DEPTH, N_EXPERTS), f32)
    w_gate_up = nrm(ks[15], (DEPTH, N_EXPERTS, D_MODEL, 2 * D_EXPERT), f32) * (D_MODEL ** -0.5)
    b_gate_up = 0.01 * nrm(ks[16], (DEPTH, N_EXPERTS, 2 * D_EXPERT), f32)
    w_down = nrm(ks[17], (DEPTH, N_EXPERTS, D_EXPERT, D_MODEL), f32) * (D_EXPERT ** -0.5) * DN_BETA
    b_down = 0.01 * nrm(ks[18], (DEPTH, N_EXPERTS, D_MODEL), f32)
    ln2_g = 1.0 + 0.02 * nrm(ks[19], (DEPTH, D_MODEL), f32)
    ln2_b = 0.02 * nrm(ks[20], (DEPTH, D_MODEL), f32)
    return {'x_prompt': x_prompt, 'x_sample': x_sample,
            'cache_k_moba': cache_k_moba, 'cache_v_moba': cache_v_moba,
            'state_k_win': state_k_win, 'state_v_win': state_v_win, 'page_table': page_table,
            'w_in': w_in, 'gn_moba': gn_moba, 'gn_win': gn_win, 'w_out': w_out,
            'ln1_g': ln1_g, 'ln1_b': ln1_b, 'w_router': w_router, 'b_router': b_router,
            'w_gate_up': w_gate_up, 'b_gate_up': b_gate_up, 'w_down': w_down, 'b_down': b_down,
            'ln2_g': ln2_g, 'ln2_b': ln2_b}

def reference(x_prompt, x_sample, cache_k_moba, cache_v_moba, state_k_win, state_v_win, page_table,
              w_in, gn_moba, gn_win, w_out, ln1_g, ln1_b, w_router, b_router,
              w_gate_up, b_gate_up, w_down, b_down, ln2_g, ln2_b):
    y_prompt, y_sample = x_prompt, x_sample
    per_layer = []
    for l in range(DEPTH):
        out = trunk_layer(y_prompt, y_sample, cache_k_moba[l], cache_v_moba[l], state_k_win[l], state_v_win[l],
                          page_table, w_in[l], gn_moba[l], gn_win[l], w_out[l], ln1_g[l], ln1_b[l],
                          w_router[l], b_router[l], w_gate_up[l], b_gate_up[l], w_down[l], b_down[l],
                          ln2_g[l], ln2_b[l])
        y_prompt, y_sample = out[0], out[1]
        per_layer.append(out[2:])
    k_moba_prompt = jnp.stack([st[0] for st in per_layer])
    v_moba_prompt = jnp.stack([st[1] for st in per_layer])
    k_moba_sample = jnp.stack([st[2] for st in per_layer])
    v_moba_sample = jnp.stack([st[3] for st in per_layer])
    k_win_prompt = jnp.stack([st[4] for st in per_layer])
    v_win_prompt = jnp.stack([st[5] for st in per_layer])
    k_win_sample = jnp.stack([st[6] for st in per_layer])
    v_win_sample = jnp.stack([st[7] for st in per_layer])
    return (y_prompt, y_sample, k_moba_prompt, v_moba_prompt, k_moba_sample, v_moba_sample,
            k_win_prompt, v_win_prompt, k_win_sample, v_win_sample)


_drawn_inputs = setup_inputs


def setup_inputs(seed=0):
    import zlib

    import numpy as np

    out = dict(_drawn_inputs(seed))
    spreads = {}
    factors = {'gn_moba': 3.794,
     'gn_win': 3.258,
     'b_router': 2.84,
     'b_gate_up': 8.0,
     'b_down': 8.0,
     'ln2_g': 2.822,
     'ln2_b': 2.949}
    for name, (base, spread) in spreads.items():
        noise = np.random.default_rng([zlib.crc32(name.encode()), seed]).standard_normal(out[name].shape)
        drawn = base * np.exp(spread * noise) if base else spread * noise
        out[name] = jnp.asarray(drawn.astype(out[name].dtype))
    for name, factor in factors.items():
        out[name] = (out[name] * factor).astype(out[name].dtype)
    return out
```

```python
from contextlib import ExitStack

import numpy as np
import concourse.bass as bass
from concourse import mybir

F32 = mybir.dt.float32
I32 = mybir.dt.int32
U32 = mybir.dt.uint32
ALU = mybir.AluOpType
ACT = mybir.ActivationFunctionType
AXX = mybir.AxisListType.X

D = 1024
KC = D // 128
SEQ = 256
DB, DS = 8, 4
NS = DB * DS
T = SEQ + NS
TILES = ((0, 128), (128, 128), (256, NS))
H, HD = 8, 64
G = 512
PAST = 256
PAGE = 128
E, TOPK = 32, 4
PAIRS = E // 2
SLOTS = 64
CHUNKS = -(-T // SLOTS)
PATTERNS = ((128, 1), (512, 4), (2048, 16))
ALPHA = 2.0 ** 0.25
SCALE = HD ** -0.5
LN_EPS, RMS_EPS = 1e-5, 1e-6
LIMIT, SWISH = 7.0, 1.702
NEG = -1e30
UNITS = 12
RING = 8
VRING, KRING = 6, 4
ORDER = (2, 0, 1)

SLOPES = [2.0 ** (-8.0 * (h + 1) / H) for h in range(H)]

C_ID, C_TRI, C_ONE, C_IOTA = 0, 128, 256, 384
C_SEL = C_IOTA + CHUNKS * SLOTS
C_HEAD = C_SEL + 8 * SLOTS
C_END = C_HEAD + H
A_DIST, A_MASK, A_SAMP = 0, 384, 384 * 3
SW = PAST + NS
A_END = A_SAMP + 4 * SW


def multiplicity(d):
    return sum((d % dil == 0) & (d <= win) for win, dil in PATTERNS)


def seen(d, group):
    n = (d >= 0) * (multiplicity(d) if group else 1)
    return np.where(n > 0, np.log(np.maximum(n, 1)), NEG).astype(np.float32)


def constant_tables():
    keep = np.zeros((128, C_END), np.float32)
    p = np.arange(128)
    keep[:, C_ID:C_ID + 128] = np.eye(128)
    keep[:, C_TRI:C_TRI + 128] = p[:, None] < p[None, :]
    keep[:, C_ONE:C_ONE + 128] = 1
    keep[:, C_IOTA:C_SEL] = np.arange(CHUNKS * SLOTS)
    for r in range(8):
        keep[r, C_SEL + r * SLOTS:C_SEL + (r + 1) * SLOTS] = 1
    keep[p, C_HEAD + p // DS % H] = 1
    att = np.zeros((128, A_END), np.float32)
    d = np.concatenate([128 + p[:, None] - np.arange(256), p[:, None] - np.arange(128)], 1)
    att[:, A_DIST:A_DIST + 384] = d
    for g in range(2):
        att[:, A_MASK + 384 * g:A_MASK + 384 * (g + 1)] = seen(d, g)
    b, h, q = p // NS, p // DS % H, p % DS
    for g in range(2):
        for quad in range(2):
            t = PAST + q[:, None]
            key = np.concatenate([np.arange(PAST), PAST + np.arange(NS) % DS])[None, :]
            dist = t - key
            s = seen(dist, g) - np.array(SLOPES)[h][:, None] * dist
            other = np.arange(NS)[None, :] // DS != 4 * quad + b[:, None]
            s[:, PAST:][other] = NEG
            at = A_SAMP + (2 * g + quad) * SW
            att[:, at:at + SW] = np.maximum(s, NEG)
    return keep, att


class Count:

    def __init__(self, sem):
        self.sem, self.n = sem, 0

    def on(self, ins, by=1):
        ins.then_inc(self.sem, by)
        self.n += by
        return self.n


def build_layer(nc, x_prompt, x_sample, cache_k, cache_v, state_k, state_v, page_table, w_in, gn_moba,
                gn_win, w_out, ln1_g, ln1_b, w_router, b_router, w_gate_up, b_gate_up, w_down, b_down,
                ln2_g, ln2_b, keep_table, att_table,
                y_prompt, y_sample, k_moba_p, v_moba_p, k_moba_s, v_moba_s,
                k_win_p, v_win_p, k_win_s, v_win_s):
    ctx = ExitStack()

    cursor = [nc.sbuf_base + (-nc.sbuf_base) % 64]

    def place(name, shape, at=None, dt=F32):
        size = 4 * int(np.prod(shape[1:]))
        if at is None:
            at = cursor[0]
            cursor[0] += size + (-size) % 32
        assert at + size <= nc.sbuf_usable_end, (name, at + size - nc.sbuf_usable_end)
        return nc.alloc_sbuf_tensor_at(name, shape, dt, offset=at)

    keep = place("keep", [128, C_END])
    ident, tri, ones = keep[:, C_ID:C_ID + 128], keep[:, C_TRI:C_TRI + 128], keep[:, C_ONE:C_ONE + 128]
    hx = place("hx", [128, 3, D])
    acc_at = cursor[0]
    acc = place("acc", [128, 3, D])
    otok = place("otok", [128, 2, D], at=acc_at)
    otS = place("otS", [128, 4, HD], at=acc_at + 8192)
    sampM = place("sampM", [128, G], at=acc_at + 9216)
    ln_g, ln_b = place("ln_g", [128, D]), place("ln_b", [128, D])
    idx_u = place("idx_u", [128, 3, 8], dt=U32)
    small = place("small", [128, 512])
    posm = place("posm", [128, 3, E])
    comb = place("comb", [128, 3, E])
    counts = place("counts", [1, 32], dt=I32)
    bias_rows = place("bias_rows", [8, 512])
    share_at = cursor[0]
    xg = place("xg", [128, KC, 2 * SLOTS])
    gate, up, sig = (place(n, [128, D]) for n in ("gate", "up", "sig"))
    actT = place("actT", [128, KC, 2 * SLOTS])
    first = place("first", [128, 4096], at=cursor[0] - 16384)
    ybuf_at = cursor[0]
    ybuf = place("ybuf", [128, D])
    pick = place("pick", [128, 3, 2 * SLOTS])
    pickw = place("pickw", [128, 3, 2 * SLOTS])
    spread_at = cursor[0]
    spread = place("spread", [128, T])
    ring_at = cursor[0]
    ring = [place(f"ring{s}", [128, 4096]) for s in range(RING)]
    cursor[0] = share_at
    att = place("att", [128, A_END])
    wrt = place("wrt", [128, KC, E], at=share_at)
    brt = place("brt", [128, E], at=share_at + 1024)
    mask3 = place("mask3", [128, 3, E], at=share_at + 1152)
    rtmp = place("rtmp", [128, 3, 2 * TOPK * E], at=acc_at)
    lg = place("lg", [128, 3, E], at=share_at + 1536)
    lgT = place("lgT", [E, T], at=share_at + 1920)
    page_sb = place("page_sb", [1, 16], dt=I32)
    gn_rows = place("gn_rows", [KC, 128])
    gnT = place("gnT", [128, KC])
    headS = place("headS", [128, 2, 384])
    upper = place("upper", [NS, 512], at=cursor[0] - 3072)
    headP = place("headP", [128, 2, 384])
    headB = place("headB", [128, 2, 384])
    headPT = place("headPT", [128, 2, 384])
    sampS = place("sampS", [128, SW])
    sampP = place("sampP", [128, SW])
    kstage = place("kstage", [128, G])
    assert cursor[0] <= ring_at
    bdn = place("bdn", [E, D], at=ybuf_at)
    combT = place("combT", [E, T], at=spread_at)
    cursor[0] = ring_at
    vring = place("vring", [128, VRING, 2, G])
    kring = place("kring", [128, KRING, 2, G])
    qkvT = place("qkvT", [128, 24, T])
    vtok = place("vtok", [128, 3, 2, G])
    qblk = place("qblk", [128, 2, DB, 4, 32])
    sampPT = place("sampPT", [128, 3, 128])
    w_at = cursor[0]
    assert w_at >= ring_at + 5 * 16384
    wblk = place("wblk", [128, 4, KC, 256])
    wout = place("wout", [128, KC, D], at=w_at)
    kT = place("kT", [128, 4, 4, PAST])
    x_at = max(cursor[0] - 4 * KC * T, ring_at + 8 * 16384)
    xT = place("xT", [128, KC, T], at=x_at)

    bank = [nc.alloc_psum_tensor(f"bank{i}", [128, 512], F32) for i in range(8)]

    names = """consts_in x_in pages_in w_in_landed0 w_in_landed1 w_in_landed2 w_in_landed3 wout_in k_landed0 k_landed1
        k_landed2 k_landed3 v_landed0 v_landed1 v_landed2 v_landed3 v_landed4 v_landed5 ln1_in router_in bdn_in
        ln2_in x_turned xT_ready projected proj_copied kv_turned vtok_ready kstage_ready kstage_stored gn_turned
        gn_ready head_scored head_summed head_maxed head_exped probs_turned probs_copied head_mixed head_taken
        keys_turned keys_copied_act keys_copied_dve samp_scored samp_summed samp_maxed samp_exped samp_scaled
        samp_turned samp_copied samp_mixed samp_taken qblk_ready rms_squared rms_summed rms_rooted outs_normed
        outs_turned outT_ready outT_scaled attended hx_varied hx_scaled hx_rooted upper_ready hx_centred
        hx_ready hx_turned hxT_ready logitsT_done logitsT_ready routed logits_used expo_ready masks_ready
        weights_ready counted comb_turned combT_ready spread_down route_ready unit0 unit1 unit2 unit3 unit4
        unit5 unit6 unit7 unit_used first_in att_in gn_in bias_in bias_used picked gathered xg_ready
        gate_up_done clipped sigmoided act_ready act_turned actT_ready pickw_turned spread_ready down_done
        y_ready mixed added y_varied y_scaled y_rooted y_centred y_gained hx_gained y_normed copies_out
        results_out dve_done pool_done dve_moe pass_added""".split()
    sems = {n: nc.alloc_semaphore(n) for n in names}
    S = type("Semaphores", (), sems)
    w_landed = [sems[f"w_in_landed{i}"] for i in range(4)]
    k_landed = [sems[f"k_landed{i}"] for i in range(KRING)]
    v_landed = [sems[f"v_landed{i}"] for i in range(VRING)]
    unit_in = [sems[f"unit{i}"] for i in range(RING)]

    xp, xs = x_prompt[0], x_sample.rearrange("b s d -> (b s) d")
    yp, ys = y_prompt[0], y_sample.rearrange("b s d -> (b s) d")
    pages_k = cache_k.rearrange("a n p h d -> (a n) p (h d)")
    pages_v = cache_v.rearrange("a n p h d -> (a n) p (h d)")
    win_k, win_v = (s.rearrange("a b (c p) h d -> (a b) p c (h d)", p=128) for s in (state_k, state_v))
    w_in_v = w_in[0].rearrange("(k p) n -> p k n", p=128)
    w_out_v = w_out[0].rearrange("(k p) n -> p k n", p=128)
    kv_out = [[(k_moba_p, k_moba_s), (v_moba_p, v_moba_s)], [(k_win_p, k_win_s), (v_win_p, v_win_s)]]

    col = [0]

    def columns(n):
        col[0] += n
        assert col[0] <= 512
        return col[0] - n

    c_max, c_sum, c_rec = columns(32), columns(32), columns(32)
    c_ssq = columns(32)
    c_smax, c_ssum, c_srec, c_sssq = columns(4), columns(4), columns(4), columns(4)
    c_stat, c_mv = columns(36), columns(12)
    c_top, c_diff, c_exp, c_tot, c_idx = columns(24), columns(12), columns(12), columns(3), columns(24)
    c_cnt = columns(20)
    c_junk = columns(64)

    def s_(c, n=1, rows=slice(0, 128)):
        return small[rows, c:c + n]

    def spread_over(ap, n):
        return ap.unsqueeze(2).broadcast_to([ap.shape[0], ap.shape[1], n])

    key_jobs = [(m // 8, m // 4 % 2, m % 4) for m in range(16)]
    tile_order = [*range(16), *range(20, 24), *range(16, 20)]
    block_order = [ft // 2 for ft in tile_order[::2]]
    copied_at = [tile_order.index(ft) + 1 for ft in range(24)]
    kv_jobs = [(0, 0, t) for t in range(3)] + [(0, 1, t) for t in range(3)] + \
              [(1, 1, t) for t in range(3)] + [(1, 0, t) for t in range(3)]
    kv_slot = []
    for g, kind, _ in kv_jobs:
        last = copied_at[12 * g + 4 * kind + 7]
        kv_slot.append(max(last, (kv_slot or [0])[-1] + 1))

    def rows_turned(n):
        kind = kv_jobs[n][1]
        return (S.kstage_ready, S.vtok_ready)[kind], sum(k2 == kind for _, k2, _ in kv_jobs[:n + 1])

    STEP0 = 14
    KEYS0 = 24 - STEP0
    STEPS = KEYS0 + 2 * 4 + 3
    assert STEPS >= 2 * H + 3

    def proj_bank(n):
        return 2 + n % 4 if n < 12 else 4 + n % 2

    def keys_at(step):
        m = 2 * (step - KEYS0)
        return (m, m + 1) if 0 <= m < 16 else ()

    def quad_at(step, lag):
        q, r = divmod(step - lag - KEYS0, 2)
        return q if r == 0 and 0 <= q < 4 else None

    def pair_of(p):
        return slice(2 * p, 2 * p + 2) if isinstance(p, int) else bass.ds(p * 2, 2)

    assert 2 * UNITS % RING == 0
    ROUNDS = 2 * UNITS // RING

    def slot_of(odd, u):
        return (UNITS * odd + u - 1) % RING

    def unit_value(m, odd, u):
        return m * (16 * ROUNDS) + 16 * ((UNITS * odd + u - 1) // RING + 1)

    LOGIT_BANK = (7, 2, 7)

    def stored_after(n):
        return 16 * sum(DB if (g, t) == (1, 2) else 1 for g in range(2) for t in range(3) if 3 * g + t < n)

    COPIES = 16 * (2 * DB + 5 + DB)

    block = ctx.enter_context(nc.Block())

    def skip(eng, sem, i, n, first=0):
        eng.wait_ge(sem, i * n + first)
        eng.sem_inc(sem, n)

    def further_passes(eng, more, none):
        eng.wait_ge(S.route_ready, 1)
        most = eng.value_load(counts[0:1, 16:17], min_val=0, max_val=T)
        with eng.If(most > SLOTS):
            with eng.Fori(1, CHUNKS) as c:
                with eng.Fori(0, PAIRS // 2) as half:
                    for odd in range(2):
                        p, m = half * 2 + odd, c * (PAIRS // 2) + half
                        n = eng.value_load(counts[0:1, bass.ds(p, 1)], min_val=0, max_val=T)
                        with eng.If(n > c * SLOTS):
                            more(c * PAIRS + p, p, c, m, odd)
                        with eng.Else():
                            none(c * PAIRS + p, m, odd)
                        eng.nop()
            eng.nop()
        with eng.Else():
            eng.nop()

    @block.sync
    def _(sp):
        for t, (t0, n) in enumerate(TILES):
            src = xp[t0:t0 + n, :] if t < 2 else xs
            sp.dma_start(hx[0:n, t, :], src).then_inc(S.x_in, 16)

        def load_w_in(n):
            if n >= 4:
                sp.wait_ge(S.projected, 2 * (n - 3))
            c = 256 * block_order[n]
            sp.dma_start(wblk[:, n % 4], w_in_v[:, :, c:c + 256]).then_inc(w_landed[n % 4], 16)

        for n in range(4):
            load_w_in(n)

        def load_keys(m, ap_of, ring_of, sem):
            g, quad, b4 = key_jobs[m]
            b = 4 * quad + b4
            if g == 0:
                for c in range(2):
                    sp.dma_start(ring_of[:, c, :], ap_of[0][bass.ds(page[2 * b + c], 1), :, :].rearrange(
                        "a p n -> p (a n)")).then_inc(sem, 16)
            else:
                for c in range(2):
                    sp.dma_start(ring_of[:, c, :], ap_of[1][b, :, c, :]).then_inc(sem, 16)

        def load_k(m):
            if m >= KRING:
                sp.wait_ge(S.keys_turned, 2 * (m - KRING + 1))
            load_keys(m, (pages_k, win_k), kring[:, m % KRING], k_landed[m % KRING])

        def load_v(m):
            if m >= VRING:
                sp.wait_ge(S.samp_mixed, (m - VRING) // 4 + 1)
            load_keys(m, (pages_v, win_v), vring[:, m % VRING], v_landed[m % VRING])

        sp.wait_ge(S.pages_in, 16)
        page = [sp.value_load(page_sb[0:1, i:i + 1], min_val=0, max_val=pages_k.shape[0] - 1) for i in range(2 * DB)]
        for m in range(KRING):
            load_k(m)
        for n in range(4, 12):
            load_w_in(n)
            if 0 <= n - 6 < VRING:
                load_v(n - 6)

        def load_unit(p, odd, u, to=None, sem=None):
            slot = slot_of(odd, u)
            dst = (ring[slot] if to is None else to)[:, :].rearrange("p (e n) -> p e n", e=2)
            if u < 8:
                src = w_gate_up[0, pair_of(p), 128 * u:128 * u + 128, :].rearrange("e p n -> p e n")
            else:
                v = 256 * (u - 8)
                src = w_down[0, pair_of(p), v:v + 256, :].rearrange("e (p c) n -> p e (c n)", c=2)
            sp.dma_start(dst, src).then_inc(unit_in[slot] if sem is None else sem, 16)

        def load_bias(p):
            src = b_gate_up[0, pair_of(p), :].rearrange("e (n c) -> (e n) c", c=512)
            sp.dma_start(bias_rows[:, :], src).then_inc(S.bias_in, 16)

        load_bias(0)
        k_next, v_next = KRING, VRING
        for ks, vs, quarter in ((4, 0, 0), (2, 0, 1), (2, 4, 2), (4, 4, 3), (0, 2, None)):
            for m in range(ks):
                load_k(k_next)
                k_next += 1
            for m in range(vs):
                load_v(v_next)
                v_next += 1
            if quarter is not None:
                sp.wait_ge(S.projected, 24)
                c = slice(2 * quarter, 2 * quarter + 2)
                sp.dma_start(wout[:, c, :], w_out_v[:, c, :]).then_inc(S.wout_in, 16)
        sp.wait_ge(S.samp_summed, 4)
        sp.wait_ge(S.head_summed, 16)
        sp.wait_ge(S.head_mixed, 16)
        sp.dma_start(wrt[:, :, :], w_router[0].rearrange("(k p) e -> p k e", p=128)).then_inc(S.router_in, 16)
        sp.dma_start(brt[:, :], b_router[0:1, :].broadcast_to([128, E])).then_inc(S.router_in, 16)
        sp.wait_ge(S.samp_mixed, 4)
        sp.wait_ge(S.copies_out, COPIES)
        for u in range(1, 3):
            load_unit(0, 0, u)
        sp.wait_ge(S.kstage_stored, stored_after(6))
        sp.dma_start(bdn[:, :], b_down[0]).then_inc(S.bdn_in, 16)
        for u in range(3, 6):
            load_unit(0, 0, u)
        sp.wait_ge(S.hx_gained, 2)
        load_unit(0, 0, 0, first, S.first_in)
        sp.wait_ge(S.attended, 4)
        for u in range(6, 8):
            load_unit(0, 0, u)
        load_unit(0, 0, 8)
        sp.wait_ge(S.hx_ready, 6)
        sp.dma_start(ln_g[:, :], ln2_g[0:1, :].broadcast_to([128, D])).then_inc(S.ln2_in, 16)
        sp.dma_start(ln_b[:, :], ln2_b[0:1, :].broadcast_to([128, D])).then_inc(S.ln2_in, 16)

        def unit_free(m, odd, u):
            before = UNITS * odd + u - RING
            if before < 0:
                m, before = m - 1, before + 2 * UNITS
            i, u = m * 2 + before // UNITS, before % UNITS
            if u == 7:
                sp.wait_ge(S.gate_up_done, i * 4 + 4)
            elif u == 11:
                sp.wait_ge(S.down_done, i + 1)
            else:
                sp.wait_ge(S.unit_used, i * (UNITS - 2) + (u + 1 if u < 7 else u))

        def load_units(m, odd, us):
            for u in us:
                unit_free(m, odd, u)
                load_unit(m * 2 + odd, odd, u)

        def next_bias(i):
            sp.wait_ge(S.bias_used, i + 1)
            load_bias(i + 1)

        load_units(0, 0, range(9, UNITS))
        next_bias(0)
        load_units(0, 1, range(UNITS))
        with sp.Fori(1, PAIRS // 2) as m:
            next_bias(m * 2 - 1)
            load_units(m, 0, range(UNITS))
            next_bias(m * 2)
            load_units(m, 1, range(UNITS))

        def more(i, p, c, m, odd):
            sp.wait_ge(S.bias_used, i)
            load_bias(p)
            for u in range(UNITS):
                unit_free(m, odd, u)
                load_unit(p, odd, u)

        def none(i, m, odd):
            sp.wait_ge(S.bias_used, i)
            sp.sem_inc(S.bias_in, 16)
            for u in range(UNITS):
                unit_free(m, odd, u)
                sp.sem_inc(unit_in[slot_of(odd, u)], 16)

        further_passes(sp, more, none)

        for nth, t in enumerate(ORDER):
            t0, n = TILES[t]
            sp.wait_ge(S.y_normed, 2 * nth + 2)
            sp.dma_start(yp[t0:t0 + n, :] if t < 2 else ys, acc[0:n, t, :]).then_inc(S.results_out, 16)
        sp.wait_ge(S.results_out, 48)
        sp.wait_ge(S.copies_out, COPIES)
        sp.wait_ge(S.kstage_stored, stored_after(6))

    @block.gpsimd
    def _(pool):
        n_k = n_v = 0
        state_rows = iter([(b, *sd) for b in range(DB) for sd in ((state_k, k_win_s), (state_v, v_win_s))])

        def copy_state(n):
            for _ in range(n):
                b, src, dst = next(state_rows)
                pool.dma_start(dst[0, b, 0:PAST].rearrange("s h d -> s (h d)"),
                               src[0, b].rearrange("s h d -> s (h d)")).then_inc(S.copies_out, 16)

        def block_queries(g):
            pool.wait_ge(S.proj_copied, copied_at[12 * g + 3])
            for j in range(4):
                for half in range(2):
                    r = slice(64 * half, 64 * half + 64)
                    nc.gpsimd.tensor_copy(
                        qblk[r, g, :, j, 8 * j + 4 * half:8 * j + 4 * half + 4],
                        qkvT[r, 12 * g + j, SEQ:T].rearrange("p (b q) -> p b q", b=DB)).then_inc(S.qblk_ready, 1)

        nc.gpsimd.memset(qblk[:], 0.0).then_inc(S.pool_done, 1)
        for n in range(5, 9):
            pool.wait_ge(S.projected, n)
            copy_state(1)
        pool.wait_ge(S.pool_done, 1)
        block_queries(0)
        for n, (g, kind, t) in enumerate(kv_jobs):
            if n == 6:
                block_queries(1)
            to_p, to_s = kv_out[g][kind]
            t0, n = TILES[t]
            if kind == 0:
                n_k += 1
                pool.wait_ge(S.kstage_ready, n_k)
                rows, sem = kstage[0:n, :], S.kstage_stored
            else:
                n_v += 1
                pool.wait_ge(S.vtok_ready, n_v)
                rows, sem = vtok[0:n, t, g, :], S.copies_out
            if t < 2:
                pool.dma_start(to_p[0, 0, t0:t0 + n].rearrange("s h d -> s (h d)"), rows).then_inc(sem, 16)
            elif g == 0:
                pool.dma_start(to_s[0].rearrange("b s h d -> (b s) (h d)"), rows).then_inc(sem, 16)
            else:
                for b in range(DB):
                    r = kstage[4 * b:4 * b + 4, :] if kind == 0 else vtok[4 * b:4 * b + 4, t, g, :]
                    pool.dma_start(to_s[0, b, PAST:PAST + DS].rearrange("s h d -> s (h d)"), r).then_inc(sem, 16)
            copy_state(1)
        def add_bias(x, t, gained, done, nth):
            n = TILES[t][1]
            for half in range(2):
                c = slice(512 * half, 512 * half + 512)
                pool.wait_ge(gained, 2 * nth + half + 1)
                nc.gpsimd.tensor_tensor(x[0:n, t, c], x[0:n, t, c], ln_b[0:n, c], ALU.add).then_inc(done, 1)

        pool.wait_ge(S.ln1_in, 32)
        for nth, t in enumerate(ORDER):
            add_bias(hx, t, S.hx_gained, S.hx_ready, nth)
        pool.wait_ge(S.ln2_in, 32)
        for nth, t in enumerate(ORDER):
            add_bias(acc, t, S.y_gained, S.y_normed, nth)

    @block.tensor
    def _(pe):
        def turn(out, in_):
            return nc.tensor.transpose(out, in_, ident[0:in_.shape[0], 0:in_.shape[0]])

        pe.wait_ge(S.consts_in, 16)
        pe.wait_ge(S.x_in, 48)
        for k in range(KC):
            if k >= 2:
                pe.wait_ge(S.xT_ready, k - 1)
            for t, (t0, n) in enumerate(TILES):
                ins = turn(bank[k % 2][:, t0:t0 + n], hx[0:n, t, 128 * k:128 * k + 128])
            ins.then_inc(S.x_turned, 1)
        pe.wait_ge(S.xT_ready, KC)

        def turn_kv(n):
            g, kind, t = kv_jobs[n]
            t0, rows = TILES[t]
            ft = 12 * g + 4 + 4 * kind
            pe.wait_ge(S.proj_copied, copied_at[ft + 3])
            if n >= 2:
                pe.wait_ge(*rows_turned(n - 2))
            elif n == 1:
                pe.wait_ge(S.gn_ready, 1)
            for j in range(4):
                ins = turn(bank[6 + n % 2][0:rows, 128 * j:128 * j + 128], qkvT[:, ft + j, t0:t0 + rows])
            ins.then_inc(S.kv_turned, 1)

        def project(n):
            blk = n // 2
            if n % 2 == 0:
                pe.wait_ge(w_landed[blk % 4], 16 * (blk // 4 + 1))
            banks = 4 if n < 12 else 2
            if n >= 4:
                pe.wait_ge(S.proj_copied, n - banks + 1)
            for k in range(KC):
                ins = nc.tensor.matmul(bank[proj_bank(n)][:, 0:T],
                                       wblk[:, blk % 4, k, 128 * (n % 2):128 * (n % 2) + 128], xT[:, k, :],
                                       start=(k == 0), stop=(k == KC - 1))
            ins.then_inc(S.projected, 1)

        def head_scores(n):
            g, h = divmod(n, H)
            r = slice(64 * (h % 2), 64 * (h % 2) + 64)
            pe.wait_ge(S.proj_copied, copied_at[12 * g + 4 + h // 2])
            q, k = qkvT[r, 12 * g + h // 2, :], qkvT[r, 12 * g + 4 + h // 2, :]
            if n >= 2:
                pe.wait_ge(S.head_summed, n - 1)
            nc.tensor.matmul(bank[n % 2][:, 0:256], q[:, 128:256], k[:, 0:256], start=True, stop=True)
            nc.tensor.matmul(bank[n % 2][:, 256:384], q[:, 0:128], k[:, 0:128],
                             start=True, stop=True).then_inc(S.head_scored, 1)

        def head_turn(n):
            pe.wait_ge(S.head_exped, 2 * n + 2)
            if n:
                pe.wait_ge(S.probs_copied, n)
            for c in range(3):
                ins = turn(bank[2][:, 128 * c:128 * c + 128], headP[:, n % 2, 128 * c:128 * c + 128])
            ins.then_inc(S.probs_turned, 1)

        def head_mix(n):
            g, h = divmod(n, H)
            pe.wait_ge(S.probs_copied, n + 1)
            pe.wait_ge(S.vtok_ready, 3 * g + 2)
            if n:
                pe.wait_ge(S.head_taken, n)
            P, out = headPT[:, n % 2, :], bank[3]
            v = [vtok[:, t, g, 64 * h:64 * h + 64] for t in range(2)]
            nc.tensor.matmul(out[:, 0:64], P[:, 256:384], v[0], start=True, stop=True)
            nc.tensor.matmul(out[:, 64:128], P[:, 0:128], v[0], start=True, stop=False)
            nc.tensor.matmul(out[:, 64:128], P[:, 128:256], v[1], start=False, stop=True).then_inc(S.head_mixed, 1)

        def turn_keys(m):
            pe.wait_ge(k_landed[m % KRING], 32 * (m // KRING + 1))
            for c in range(2):
                if m:
                    pe.wait_ge((S.keys_copied_act, S.keys_copied_dve)[c], m)
                else:
                    pe.wait_ge(S.proj_copied, 24)
                for j in range(4):
                    ins = turn(bank[4 + c][:, 128 * j:128 * j + 128], kring[:, m % KRING, c, 128 * j:128 * j + 128])
                ins.then_inc(S.keys_turned, 1)

        def samp_scores(q):
            g, quad = divmod(q, 2)
            if q:
                pe.wait_ge(S.samp_summed, q)
            else:
                pe.wait_ge(S.kstage_ready, 6)
                pe.wait_ge(S.vtok_ready, 6)
                pe.wait_ge(S.qblk_ready, 16)
            pe.wait_ge(S.keys_copied_act, 4 * q + 4)
            pe.wait_ge(S.keys_copied_dve, 4 * q + 4)
            for part in range(2):
                for j in range(4):
                    for b4 in range(4):
                        out = bank[6][32 * b4:32 * b4 + 32, 0:PAST] if part == 0 else bank[6][32 * b4:32 * b4 + 32, PAST:SW]
                        k = kT[:, b4, j, :] if part == 0 else qkvT[:, 12 * g + 4 + j, SEQ:T]
                        ins = nc.tensor.matmul(out, qblk[:, g, 4 * quad + b4, j, :], k, start=(j == 0), stop=(j == 3),
                                               tile_position=(0, 32 * b4))
            ins.then_inc(S.samp_scored, 1)

        def samp_turn(q):
            pe.wait_ge(S.samp_scaled, q + 1)
            if q:
                pe.wait_ge(S.samp_taken, q)
            turn(bank[7][:, 0:128], sampP[:, 0:128])
            turn(bank[7][:, 128:256], sampP[:, 128:256])
            turn(bank[7][0:NS, 256:384], sampP[:, 256:SW]).then_inc(S.samp_turned, 1)

        def samp_mix(q):
            g = q // 2
            pe.wait_ge(S.samp_copied, 2 * q + 2)
            for b4 in range(4):
                m = 4 * q + b4
                pe.wait_ge(v_landed[m % VRING], 32 * (m // VRING + 1))
            for c in range(3):
                for b4 in range(4):
                    p = slice(32 * b4, 32 * b4 + 32)
                    lhs = sampPT[:, c, p] if c < 2 else sampPT[0:NS, 2, p]
                    rhs = vring[:, (4 * q + b4) % VRING, c, :] if c < 2 else vtok[0:NS, 2, g, :]
                    ins = nc.tensor.matmul(bank[7][p, :], lhs, rhs, start=(c == 0), stop=(c == 2),
                                           tile_position=(0, 32 * b4))
            ins.then_inc(S.samp_mixed, 1)

        for slot in range(STEP0 + STEPS):
            if slot < 24:
                project(slot)
            if slot == 1:
                pe.wait_ge(S.gn_in, 32)
                turn(bank[7][:, 0:KC], gn_rows[:, :]).then_inc(S.gn_turned, 1)
            if slot in kv_slot:
                turn_kv(kv_slot.index(slot))
            s = slot - STEP0
            keys = keys_at(s)
            if 0 <= s < 2 * H:
                head_scores(s)
            if quad_at(s, 2) is not None:
                samp_scores(quad_at(s, 2))
            if keys:
                turn_keys(keys[0])
            if 1 <= s <= 2 * H:
                head_turn(s - 1)
            if keys:
                turn_keys(keys[1])
            if 2 <= s <= 2 * H + 1:
                head_mix(s - 2)
            if quad_at(s, 4) is not None:
                samp_mix(quad_at(s, 4))
            if quad_at(s, 3) is not None:
                samp_turn(quad_at(s, 3))

        pe.wait_ge(S.outs_normed, 1)
        for k in range(KC):
            if k >= 2:
                pe.wait_ge(S.outT_ready, k - 1)
            turn(bank[k % 2][:, 0:128], otok[:, 0, 128 * k:128 * k + 128])
            turn(bank[k % 2][:, 128:256], otok[:, 1, 128 * k:128 * k + 128]).then_inc(S.outs_turned, 1)
        pe.wait_ge(S.outs_normed, 2)
        for q in range(4):
            turn(bank[2 + q][0:64, 0:128], otS[:, q, :]).then_inc(S.outs_turned, 1)
        pe.wait_ge(S.wout_in, 64)

        def out_product(t, between=()):
            t0, rows = TILES[t]
            order = [(k, half) for half in range(2) for k in range(KC)] if t == 1 else \
                    [(k, half) for k in range(KC) for half in range(2)]
            for n, (k, half) in enumerate(order):
                out = bank[6 + half][NS * half:NS * half + NS, :] if t == 2 else bank[2 + 2 * t + half]
                ins = nc.tensor.matmul(out[:, :], xT[:, k, t0:t0 + rows], wout[:, k, 512 * half:512 * half + 512],
                                       start=(k == 0), stop=(k == KC - 1))
                if n == 15 or (t, n) == (1, 7):
                    ins.then_inc(S.attended, 1)
                if between and n in (10, 12, 14):
                    between[(n - 10) // 2]()

        def turn_hx(nth):
            t = ORDER[nth]
            rows = TILES[t][1]
            for a in range(2):
                pe.wait_ge(S.hx_ready, 2 * nth + a + 1)
                if nth:
                    pe.wait_ge(S.hxT_ready, 2 * nth)
                for k in range(4 * a, 4 * a + 4):
                    ins = turn(bank[a][:, 128 * (k % 4):128 * (k % 4) + rows], hx[0:rows, t, 128 * k:128 * k + 128])
                ins.then_inc(S.hx_turned, 1)

        def logits_product(nth):
            t0, rows = TILES[ORDER[nth]]
            if nth == 0:
                pe.wait_ge(S.router_in, 32)
                pe.wait_ge(S.upper_ready, 1)
            for k in range(KC):
                if k % 4 == 0:
                    pe.wait_ge(S.hxT_ready, 2 * nth + k // 4 + 1)
                ins = nc.tensor.matmul(bank[6][0:E, t0:t0 + rows], wrt[:, k, :], xT[:, k, t0:t0 + rows],
                                       start=(k == 0), stop=(k == KC - 1))
            ins.then_inc(S.logitsT_done, 1)

        def turn_logits(nth):
            t = ORDER[nth]
            t0, rows = TILES[t]
            pe.wait_ge(S.logitsT_ready, nth + 1)
            turn(bank[LOGIT_BANK[nth]][0:rows, E * t:E * t + E], lgT[:, t0:t0 + rows]).then_inc(S.routed, 1)

        def stages(nth):
            return [lambda f=f: f(nth) for f in (turn_hx, logits_product, turn_logits)]

        pe.wait_ge(S.outT_scaled, 1)
        out_product(2)
        pe.wait_ge(S.outT_ready, KC)
        out_product(0, stages(0))
        out_product(1, stages(1))
        for stage in stages(2):
            stage()
        pe.wait_ge(S.masks_ready, 3)
        for t, (t0, rows) in enumerate(TILES):
            for s in range(t + 1):
                r = TILES[s][1]
                lhs = (tri if s == t else ones)[0:r, 0:rows]
                nc.tensor.matmul(bank[3][0:rows, E * t:E * t + E], lhs, mask3[0:r, s, :], start=(s == 0), stop=(s == t))
        for s in range(3):
            r = TILES[s][1]
            ins = nc.tensor.matmul(bank[3][0:32, 3 * E:4 * E], ones[0:r, 0:32], mask3[0:r, s, :], start=(s == 0), stop=(s == 2))
        ins.then_inc(S.counted, 1)

        def turn_comb():
            pe.wait_ge(S.weights_ready, 3)
            for t, (t0, rows) in enumerate(TILES):
                ins = turn(bank[4][0:E, t0:t0 + rows], comb[0:rows, t, :])
            ins.then_inc(S.comb_turned, 1)

        def add_biases():
            pe.wait_ge(S.combT_ready, 1)
            pe.wait_ge(S.bdn_in, 16)
            for j in range(6):
                t, half = divmod(j, 2)
                t0, rows = TILES[t]
                if j >= 2:
                    pe.wait_ge(S.added, j - 1)
                nc.tensor.matmul(bank[4 + half][0:rows, :], combT[:, t0:t0 + rows],
                                 bdn[:, 512 * half:512 * half + 512], start=True, stop=True).then_inc(S.spread_down, 1)

        def gather(i, turned_before):
            pe.wait_ge(S.picked, i * 2 + 1)
            if turned_before is not None:
                pe.wait_ge(S.actT_ready, turned_before)
            for a in range(2):
                for k in range(4 * a, 4 * a + 4):
                    for t, (t0, rows) in enumerate(TILES):
                        ins = nc.tensor.matmul(bank[6 + a][:, 128 * (k % 4):128 * (k % 4) + 128],
                                               hx[0:rows, t, 128 * k:128 * k + 128], pick[0:rows, t, :],
                                               start=(t == 0), stop=(t == 2))
                ins.then_inc(S.gathered, 1)

        def gate_up(i, m, odd, between={}):
            pe.wait_ge(S.xg_ready, i * 2 + 2)
            pe.wait_ge(S.act_ready, i * 4)
            pe.wait_ge(S.bias_in, i * 16 + 16)
            for n in range(4):
                for e in range(2):
                    ins = nc.tensor.matmul(bank[n][64 * e:64 * e + 64, :],
                                           keep[0:8, C_SEL + SLOTS * (4 * e + n):C_SEL + SLOTS * (4 * e + n + 1)],
                                           bias_rows[:, :], start=True, stop=False)
            ins.then_inc(S.bias_used, 1)
            for k in range(KC):
                w = ring[slot_of(odd, k)]
                if isinstance(i, int) and i == 0 and k == 0:
                    w = first
                    pe.wait_ge(S.first_in, 16)
                else:
                    pe.wait_ge(unit_in[slot_of(odd, k)], unit_value(m, odd, k))
                for n in range(4):
                    for e in range(2):
                        ins = nc.tensor.matmul(bank[n][64 * e:64 * e + 64, :], xg[:, k, 64 * e:64 * e + 64],
                                               w[:, 2048 * e + 512 * n:2048 * e + 512 * n + 512],
                                               start=False, stop=(k == KC - 1))
                    if k == KC - 1:
                        ins.then_inc(S.gate_up_done, 1)
                if k < KC - 1:
                    ins.then_inc(S.unit_used, 1)
                if k in between:
                    between[k]()

        def turn_weights(i, copied_before):
            pe.wait_ge(S.picked, i * 2 + 2)
            pe.wait_ge(S.xg_ready, copied_before)
            for t, (t0, rows) in enumerate(TILES):
                ins = turn(bank[6][:, t0:t0 + rows], pickw[0:rows, t, :])
            ins.then_inc(S.pickw_turned, 1)

        def turn_act(i, copied_before):
            for a in range(2):
                pe.wait_ge(S.act_ready, i * 4 + (2 * a + 2))
                if a == 0:
                    pe.wait_ge(S.xg_ready, copied_before)
                else:
                    pe.wait_ge(S.spread_ready, i + 1)
                for j in range(4 * a, 4 * a + 4):
                    f = 256 * (j // 2)
                    ins = turn(bank[7 - a][:, 128 * (j % 4):128 * (j % 4) + 128], up[:, f + j % 2:f + 256:2])
                ins.then_inc(S.act_turned, 1)

        def down(i, m, odd):
            pe.wait_ge(S.added, i * 6 + 6)
            for v in range(4):
                u = 8 + v
                w = ring[slot_of(odd, u)]
                pe.wait_ge(unit_in[slot_of(odd, u)], unit_value(m, odd, u))
                pe.wait_ge(S.actT_ready, i * 2 + (1 if v < 2 else 2))
                for c in range(2):
                    j = 2 * v + c
                    for half in range(2):
                        for e in range(2):
                            at = 2048 * e + 1024 * c + 512 * half
                            ins = nc.tensor.matmul(bank[4 + half][64 * e:64 * e + 64, :], actT[:, j, 64 * e:64 * e + 64],
                                                   w[:, at:at + 512], start=(j == 0), stop=(j == KC - 1))
                if v < 3:
                    ins.then_inc(S.unit_used, 1)
            ins.then_inc(S.down_done, 1)

        def combine(i):
            pe.wait_ge(S.y_ready, i * 2 + 2)
            pe.wait_ge(S.spread_ready, i + 1)
            for j in range(6):
                t, half = divmod(j, 2)
                t0, rows = TILES[t]
                if j >= 2:
                    pe.wait_ge(S.added, i * 6 + (6 + j - 1))
                nc.tensor.matmul(bank[4 + half][0:rows, :], spread[:, t0:t0 + rows], ybuf[:, 512 * half:512 * half + 512],
                                 start=True, stop=True).then_inc(S.mixed, 1)

        def finish(i, m, odd, m_next):
            gather(i + 1, i * 2)
            turn_weights(i, i * 2 + 3)
            turn_act(i, i * 2 + 4)
            down(i, m, odd)
            gate_up(i + 1, m_next, 1 - odd, {3: lambda: combine(i)})

        gather(0, None)
        pe.wait_ge(S.route_ready, 1)
        gate_up(0, 0, 0, {1: turn_comb, 3: add_biases})
        with pe.Fori(0, PAIRS // 2 - 1) as m:
            finish(m * 2, m, 0, m)
            finish(m * 2 + 1, m, 1, m + 1)
        last = PAIRS - 1
        finish(last - 1, last // 2, 0, last // 2)
        turn_weights(last, 2 * last + 1)
        turn_act(last, 2 * last + 2)
        down(last, last // 2, 1)
        combine(last)

        def more(i, p, c, m, odd):
            gather(i, i * 2)
            gate_up(i, m, odd)
            turn_weights(i, i * 2 + 1)
            turn_act(i, i * 2 + 2)
            down(i, m, odd)
            combine(i)

        def none(i, m, odd):
            for sem, n in ((S.gathered, 2), (S.bias_used, 1), (S.unit_used, UNITS - 2), (S.gate_up_done, 4),
                           (S.pickw_turned, 1), (S.act_turned, 2), (S.down_done, 1), (S.mixed, 6)):
                skip(pe, sem, i, n)

        further_passes(pe, more, none)

    @block.scalar
    def _(act):
        act.dma_start(keep[:, :], keep_table).then_inc(S.consts_in, 16)
        act.dma_start(page_sb[:, :], page_table.rearrange("b j -> (b j)").unsqueeze(0)).then_inc(S.pages_in, 16)
        act.dma_start(gn_rows[0:4, :], gn_moba.rearrange("a (k p) -> (a k) p", p=128)).then_inc(S.gn_in, 16)
        act.dma_start(gn_rows[4:8, :], gn_win.rearrange("a (k p) -> (a k) p", p=128)).then_inc(S.gn_in, 16)

        def copy(out, in_, **kw):
            return nc.scalar.activation(out, in_, ACT.Copy, **kw)

        def k_rows(n):
            g, kind, t = kv_jobs[n]
            rows = TILES[t][1]
            done = 3 * g + t
            act.wait_ge(S.kv_turned, n + 1)
            if done:
                act.wait_ge(S.kstage_stored, stored_after(done))
            copy(kstage[0:rows, :], bank[6 + n % 2][0:rows, :]).then_inc(S.kstage_ready, 1)

        def copy_keys(m):
            act.wait_ge(S.keys_turned, 2 * m + 1)
            if m >= 4:
                act.wait_ge(S.samp_scored, m // 4)
            copy(kT[:, m % 4, :, 0:128], bank[4][:, :].rearrange("p (j c) -> p j c", j=4)).then_inc(S.keys_copied_act, 1)

        for slot in range(STEP0 + STEPS):
            if slot < 24:
                act.wait_ge(S.projected, slot + 1)
                copy(qkvT[:, tile_order[slot], :], bank[proj_bank(slot)][:, 0:T]).then_inc(S.proj_copied, 1)
            if slot == 3:
                act.dma_start(att[:, :], att_table).then_inc(S.att_in, 16)
            if slot == 5:
                act.dma_start(ln_g[:, :], ln1_g[0:1, :].broadcast_to([128, D])).then_inc(S.ln1_in, 16)
                act.dma_start(ln_b[:, :], ln1_b[0:1, :].broadcast_to([128, D])).then_inc(S.ln1_in, 16)
            if slot in kv_slot and kv_jobs[kv_slot.index(slot)][1] == 0:
                k_rows(kv_slot.index(slot))
            s = slot - STEP0
            keys = keys_at(s)
            if keys:
                copy_keys(keys[0])
            if 0 <= s < 2 * H:
                act.wait_ge(S.head_maxed, 2 * s + 2)
                if s >= 2:
                    act.wait_ge(S.probs_turned, s - 1)
                for t, cols in ((0, slice(256, 384)), (1, slice(0, 256))):
                    nc.scalar.activation(headP[:, s % 2, cols], headS[:, s % 2, cols], ACT.Exp, bias=s_(c_max + 2 * s + t),
                                         accum_out=s_(c_sum + 2 * s + t)).then_inc(S.head_exped, 1)
            if keys:
                copy_keys(keys[1])
            if 1 <= s <= 2 * H:
                m = s - 1
                act.wait_ge(S.probs_turned, m + 1)
                if m >= 2:
                    act.wait_ge(S.head_mixed, m - 1)
                copy(headPT[:, m % 2, :], bank[2][:, 0:384]).then_inc(S.probs_copied, 1)
            if 3 <= s <= 2 * H + 2:
                m = s - 3
                act.wait_ge(S.head_taken, m + 1)
                for t in range(2):
                    if m or t:
                        act.wait_ge(S.rms_squared, 2 * m + t)
                    nc.scalar.activation(s_(c_junk, 64), otok[:, t, 64 * m:64 * m + 64], ACT.Square,
                                         accum_out=s_(c_ssq + 16 * t + m)).then_inc(S.rms_squared, 1)
            q = quad_at(s, 3)
            if q is not None:
                act.wait_ge(S.samp_turned, q + 1)
                if q:
                    act.wait_ge(S.samp_mixed, q)
                copy(sampPT[:, 0:2, :], bank[7][:, 0:256].rearrange("p (c q) -> p c q", c=2)).then_inc(S.samp_copied, 1)
                copy(sampPT[0:NS, 2, :], bank[7][0:NS, 256:384]).then_inc(S.samp_copied, 1)
            q = quad_at(s, 2)
            if q is not None:
                act.wait_ge(S.samp_maxed, q + 1)
                if q:
                    act.wait_ge(S.samp_turned, q)
                nc.scalar.activation(sampP[:, :], sampS[:, :], ACT.Exp, bias=s_(c_smax + q),
                                     accum_out=s_(c_ssum + q)).then_inc(S.samp_exped, 1)

        for n in range(2):
            act.wait_ge(S.rms_summed, n + 1)
            a = s_(c_ssq, 32) if n == 0 else s_(c_sssq, 4)
            nc.scalar.activation(a, a, ACT.Sqrt).then_inc(S.rms_rooted, 1)
        for k in range(KC):
            act.wait_ge(S.outs_turned, k + 1)
            copy(xT[:, k, 0:SEQ], bank[k % 2][:, 0:SEQ], scale=gnT[:, k:k + 1]).then_inc(S.outT_ready, 1)

        def root(t, varied, rooted, nth):
            mv = s_(c_mv + 4 * t, 4, slice(0, TILES[t][1]))
            act.wait_ge(varied, nth + 1)
            nc.scalar.activation(mv[:, 1:2], mv[:, 1:2], ACT.Sqrt).then_inc(rooted, 1)

        def normalise(x, t, scaled, centred, nth):
            n = TILES[t][1]
            mv = s_(c_mv + 4 * t, 4, slice(0, n))
            act.wait_ge(scaled, nth + 1)
            for half in range(2):
                c = slice(512 * half, 512 * half + 512)
                nc.scalar.activation(x[0:n, t, c], x[0:n, t, c], ACT.Identity, bias=mv[:, 2:3],
                                     scale=mv[:, 1:2]).then_inc(centred, 1)

        def copy_logits(nth):
            t0, rows = TILES[ORDER[nth]]
            for a in range(2):
                act.wait_ge(S.hx_turned, 2 * nth + a + 1)
                copy(xT[:, 4 * a:4 * a + 4, t0:t0 + rows],
                     bank[a][:, :].rearrange("p (k c) -> p k c", k=4)[:, :, 0:rows]).then_inc(S.hxT_ready, 1)
            act.wait_ge(S.logitsT_done, nth + 1)
            copy(lgT[:, t0:t0 + rows], bank[6][0:E, t0:t0 + rows]).then_inc(S.logitsT_ready, 1)

        act.wait_ge(S.attended, 1)
        copy(upper[:, :], bank[7][NS:2 * NS, :]).then_inc(S.upper_ready, 1)
        for nth, t in enumerate(ORDER):
            root(t, S.hx_varied, S.hx_rooted, nth)
            normalise(hx, t, S.hx_scaled, S.hx_centred, nth)
            copy_logits(nth)
        act.wait_ge(S.logits_used, 3)
        nc.scalar.activation(s_(c_exp, 12), s_(c_diff, 12), ACT.Exp).then_inc(S.expo_ready, 1)

        def take_gathered(i):
            for a in range(2):
                act.wait_ge(S.gathered, i * 2 + (a + 1))
                copy(xg[:, 4 * a:4 * a + 4, :], bank[6 + a][:, :].rearrange("p (k s) -> p k s", k=4)).then_inc(S.xg_ready, 1)

        def sigmoids(i):
            for n in range(4):
                c = slice(256 * n, 256 * n + 256)
                act.wait_ge(S.clipped, i * 4 + (n + 1))
                nc.scalar.activation(sig[:, c], gate[:, c], ACT.Sigmoid, scale=SWISH).then_inc(S.sigmoided, 1)

        def take_turned(i):
            act.wait_ge(S.pickw_turned, i + 1)
            copy(spread[:, :], bank[6][:, 0:T]).then_inc(S.spread_ready, 1)
            for a in range(2):
                act.wait_ge(S.act_turned, i * 2 + (a + 1))
                copy(actT[:, 4 * a:4 * a + 4, :], bank[7 - a][:, :].rearrange("p (k s) -> p k s", k=4)).then_inc(
                    S.actT_ready, 1)

        def take_down(i):
            act.wait_ge(S.down_done, i + 1)
            for half in range(2):
                copy(ybuf[:, 512 * half:512 * half + 512], bank[4 + half][:, :]).then_inc(S.y_ready, 1)

        take_gathered(0)
        act.wait_ge(S.comb_turned, 1)
        copy(combT[:, :], bank[4][0:E, 0:T]).then_inc(S.combT_ready, 1)
        sigmoids(0)
        with act.Fori(0, PAIRS - 1) as i:
            take_gathered(i + 1)
            take_turned(i)
            take_down(i)
            sigmoids(i + 1)
        take_turned(PAIRS - 1)
        take_down(PAIRS - 1)

        def more(i, p, c, m, odd):
            take_gathered(i)
            sigmoids(i)
            take_turned(i)
            take_down(i)

        def none(i, m, odd):
            for sem, n in ((S.xg_ready, 2), (S.sigmoided, 4), (S.spread_ready, 1), (S.actT_ready, 2), (S.y_ready, 2)):
                skip(act, sem, i, n)

        further_passes(act, more, none)
        for nth in range(2):
            root(ORDER[nth], S.y_varied, S.y_rooted, nth)
        for nth, t in enumerate(ORDER):
            normalise(acc, t, S.y_scaled, S.y_centred, nth)
            if nth == 0:
                root(ORDER[2], S.y_varied, S.y_rooted, 2)

    @block.vector
    def _(dve):
        step = Count(S.dve_done)

        def link(ins):
            dve.wait_ge(step.sem, step.on(ins))

        V = nc.vector
        link(V.memset(small[:, :], 0.0))
        link(V.memset(posm[:, :, :], 0.0))
        link(V.memset(comb[:, :, :], 0.0))
        for k in range(KC):
            dve.wait_ge(S.x_turned, k + 1)
            V.tensor_copy(xT[:, k, :], bank[k % 2][:, 0:T]).then_inc(S.xT_ready, 1)
        dve.wait_ge(S.gn_turned, 1)
        V.tensor_copy(gnT[:, :], bank[7][:, 0:KC]).then_inc(S.gn_ready, 1)

        def v_rows(n):
            g, kind, t = kv_jobs[n]
            rows = TILES[t][1]
            dve.wait_ge(S.kv_turned, n + 1)
            V.tensor_copy(vtok[0:rows, t, g, :], bank[6 + n % 2][0:rows, :]).then_inc(S.vtok_ready, 1)

        def head_front(n):
            g, h = divmod(n, H)
            s = n % 2
            link(V.scalar_tensor_tensor(headB[:, s, :], att[:, A_DIST:A_DIST + 384], -SLOPES[h],
                                        att[:, A_MASK + 384 * g:A_MASK + 384 * g + 384], ALU.mult, ALU.add))
            dve.wait_ge(S.head_scored, n + 1)
            if n >= 2:
                dve.wait_ge(S.head_exped, 2 * n - 2)
            V.scalar_tensor_tensor(headS[:, s, :], bank[s][:, 0:384], SCALE, headB[:, s, :],
                                   ALU.mult, ALU.add).then_inc(S.head_summed, 1)
            dve.wait_ge(S.head_summed, n + 1)
            for t, cols in ((0, slice(256, 384)), (1, slice(0, 256))):
                V.tensor_reduce(s_(c_max + 2 * n + t), headS[:, s, cols], AXX, ALU.max, negate=True).then_inc(S.head_maxed, 1)

        def head_back(n):
            s = n % 2
            dve.wait_ge(S.head_exped, 2 * n + 2)
            link(V.reciprocal(s_(c_rec + 2 * n, 2), s_(c_sum + 2 * n, 2)))
            dve.wait_ge(S.head_mixed, n + 1)
            link(V.tensor_scalar(otok[:, 0, 64 * n:64 * n + 64], bank[3][:, 0:64], s_(c_rec + 2 * n), None, ALU.mult))
            V.tensor_scalar(otok[:, 1, 64 * n:64 * n + 64], bank[3][:, 64:128], s_(c_rec + 2 * n + 1), None,
                            ALU.mult).then_inc(S.head_taken, 1)

        def rms(a, o, nth, sem):
            link(V.tensor_scalar(a, a, 1.0 / HD, RMS_EPS, ALU.mult, ALU.add))
            dve.sem_inc(S.rms_summed, 1)
            dve.wait_ge(S.rms_rooted, nth)
            link(V.reciprocal(a, a))
            V.tensor_tensor(o, o, spread_over(a, HD), ALU.mult).then_inc(sem, 1)

        def rms_of_prompt():
            dve.wait_ge(S.rms_squared, 32)
            rms(s_(c_ssq, 32), otok[:, :, :].rearrange("p t (h d) -> p (t h) d", h=2 * H), 1, S.outs_normed)

        heads = keep[:, C_HEAD:C_HEAD + H]

        def copy_keys(m):
            dve.wait_ge(S.keys_turned, 2 * m + 2)
            if m >= 4:
                dve.wait_ge(S.samp_scored, m // 4)
            V.tensor_copy(kT[:, m % 4, :, 128:256], bank[5][:, :].rearrange(
                "p (j c) -> p j c", j=4)).then_inc(S.keys_copied_dve, 1)

        for slot in range(STEP0 + STEPS):
            if slot in kv_slot and kv_jobs[kv_slot.index(slot)][1] == 1:
                v_rows(kv_slot.index(slot))
            s = slot - STEP0
            if s == 0:
                dve.wait_ge(S.consts_in, 16)
                dve.wait_ge(S.att_in, 16)
            q = quad_at(s, 3)
            if q is not None:
                dve.wait_ge(S.samp_exped, q + 1)
                link(V.reciprocal(s_(c_srec + q), s_(c_ssum + q)))
                V.tensor_scalar(sampP[:, :], sampP[:, :], s_(c_srec + q), None, ALU.mult).then_inc(S.samp_scaled, 1)
            if 0 <= s < 2 * H:
                head_front(s)
            for m in keys_at(s):
                copy_keys(m)
            if 2 <= s <= 2 * H + 1:
                head_back(s - 2)
            q = quad_at(s, 2)
            if q is not None:
                dve.wait_ge(S.samp_scored, q + 1)
                if q:
                    dve.wait_ge(S.samp_exped, q)
                V.scalar_tensor_tensor(sampS[:, :], bank[6][:, 0:SW], SCALE,
                                       att[:, A_SAMP + SW * q:A_SAMP + SW * (q + 1)], ALU.mult, ALU.add).then_inc(S.samp_summed, 1)
                dve.wait_ge(S.samp_summed, q + 1)
                V.tensor_reduce(s_(c_smax + q), sampS[:, :], AXX, ALU.max, negate=True).then_inc(S.samp_maxed, 1)
            if s == 2 * H + 3:
                rms_of_prompt()
            q = quad_at(s, 4)
            if q is not None:
                dve.wait_ge(S.samp_mixed, q + 1)
                V.tensor_tensor(sampM[:, :].rearrange("p (h d) -> p h d", h=H),
                                bank[7][:, :].rearrange("p (h d) -> p h d", h=H), spread_over(heads, HD),
                                ALU.mult).then_inc(S.samp_taken, 1)
                dve.wait_ge(S.samp_taken, q + 1)
                link(V.tensor_reduce(otS[:, q, :], sampM[:, :].rearrange("p (h d) -> p d h", h=H), AXX, ALU.add))

        link(V.tensor_tensor(sampM[:, 0:256], otS[:, :, :].rearrange("p q d -> p (q d)"),
                             otS[:, :, :].rearrange("p q d -> p (q d)"), ALU.mult))
        link(V.tensor_reduce(s_(c_sssq, 4), sampM[:, 0:256].rearrange("p (q d) -> p q d", q=4), AXX, ALU.add))
        rms(s_(c_sssq, 4), otS[:, :, :], 2, S.outs_normed)
        for q in range(4):
            g, quad = divmod(q, 2)
            dve.wait_ge(S.outs_turned, KC + q + 1)
            src = bank[2 + q][0:64, 0:128].rearrange("p (b j r q) -> p r j b q", b=4, j=4, r=2)
            for r in range(2):
                dst = xT[64 * r:64 * r + 64, 4 * g:4 * g + 4, SEQ + 16 * quad:SEQ + 16 * quad + 16]
                ins = V.tensor_copy(dst.rearrange("p j (b q) -> p j b q", b=4), src[:, r])
                step.on(ins)
        dve.wait_ge(step.sem, step.n)
        V.tensor_tensor(xT[:, :, SEQ:T], xT[:, :, SEQ:T], spread_over(gnT[:, :], NS), ALU.mult).then_inc(S.outT_scaled, 1)

        def variance(t, varied):
            n = TILES[t][1]
            mv = s_(c_mv + 4 * t, 4, slice(0, n))
            link(V.bn_aggr(mv[:, 0:2], s_(c_stat + 12 * t, 12, slice(0, n)).rearrange("p (a c) -> p a c", a=2)))
            V.tensor_scalar(mv[:, 1:2], mv[:, 1:2], LN_EPS, None, ALU.add).then_inc(varied, 1)

        def scales(t, nth, rooted, scaled):
            mv = s_(c_mv + 4 * t, 4, slice(0, TILES[t][1]))
            dve.wait_ge(rooted, nth + 1)
            link(V.reciprocal(mv[:, 1:2], mv[:, 1:2]))
            V.scalar_tensor_tensor(mv[:, 2:3], mv[:, 0:1], -1.0, mv[:, 1:2], ALU.mult, ALU.mult).then_inc(scaled, 1)

        def gain(x, t, nth, centred, gained):
            n = TILES[t][1]
            for half in range(2):
                c = slice(512 * half, 512 * half + 512)
                dve.wait_ge(centred, 2 * nth + half + 1)
                V.tensor_tensor(x[0:n, t, c], x[0:n, t, c], ln_g[0:n, c], ALU.mult).then_inc(gained, 1)

        def attended(nth):
            t = ORDER[nth]
            n = TILES[t][1]
            if t == 2:
                dve.wait_ge(S.upper_ready, 1)
            for half in range(2):
                dve.wait_ge(S.attended, nth + 1 + (half if t == 1 else 0))
                c = slice(512 * half, 512 * half + 512)
                o = bank[2 + 2 * t + half][0:n, :] if t < 2 else (bank[6][0:n, :], upper[:, :])[half]
                link(V.scalar_tensor_tensor(hx[0:n, t, c], hx[0:n, t, c], ALPHA, o, ALU.mult, ALU.add))
                link(V.bn_stats(s_(c_stat + 12 * t + 6 * half, 6, slice(0, n)), hx[0:n, t, c]))
            variance(t, S.hx_varied)
            scales(t, nth, S.hx_rooted, S.hx_scaled)
            gain(hx, t, nth, S.hx_centred, S.hx_gained)

        top = s_(c_top, 24).rearrange("p (t k) -> p t k", t=3)
        diff = s_(c_diff, 12).rearrange("p (t k) -> p t k", t=3)
        expo = s_(c_exp, 12).rearrange("p (t k) -> p t k", t=3)
        idx = s_(c_idx, 24).rearrange("p (t k) -> p t k", t=3)

        chosen, weighted = (rtmp[:, :, a * TOPK * E:(a + 1) * TOPK * E].rearrange("p t (k e) -> p t k e", k=TOPK)
                            for a in range(2))

        def choose(nth):
            t = ORDER[nth]
            n = TILES[t][1]
            dve.wait_ge(S.routed, nth + 1)
            link(V.tensor_tensor(lg[0:n, t, :], bank[LOGIT_BANK[nth]][0:n, E * t:E * t + E], brt[0:n, :], ALU.add))
            link(V.max(top[:, t, :], lg[:, t, :]))
            V.tensor_tensor(diff[:, t, :], top[:, t, 0:TOPK], top[:, t, 0:1].broadcast_to([128, TOPK]),
                            ALU.subtract).then_inc(S.logits_used, 1)
            link(V.max_index(idx_u[:, t, :], top[:, t, :], lg[:, t, :]))
            link(V.tensor_copy(idx[:, t, :], idx_u[:, t, :]))
            link(V.tensor_tensor(chosen[:, t], keep[:, C_IOTA:C_IOTA + E].unsqueeze(1).broadcast_to([128, TOPK, E]),
                                 spread_over(idx[:, t, 0:TOPK], E), ALU.is_equal))
            V.tensor_reduce(mask3[:, t, :], chosen[:, t].rearrange("p k e -> p e k"), AXX, ALU.add).then_inc(S.masks_ready, 1)
            dve.wait_ge(S.masks_ready, nth + 1)
            link(V.tensor_scalar(posm[0:n, t, :], mask3[0:n, t, :], -4096.0, 4096.0, ALU.mult, ALU.add))

        def slot_numbers():
            dve.wait_ge(S.counted, 1)
            places = bank[3][:, 0:2 * E].rearrange("p (t e) -> p t e", t=2)
            step.on(V.tensor_tensor(posm[:, 0:2, :], posm[:, 0:2, :], places, ALU.add))
            step.on(V.tensor_tensor(posm[0:NS, 2, :], posm[0:NS, 2, :], bank[3][0:NS, 2 * E:3 * E], ALU.add))
            dve.wait_ge(step.sem, step.n)

        def weights():
            tot = s_(c_tot, 3)
            dve.wait_ge(S.expo_ready, 1)
            link(V.tensor_reduce(tot, expo, AXX, ALU.add))
            link(V.reciprocal(tot, tot))
            link(V.tensor_tensor(expo, expo, spread_over(tot, TOPK), ALU.mult))
            for t in range(3):
                step.on(V.tensor_tensor(weighted[:, t], chosen[:, t], spread_over(expo[:, t, :], E), ALU.mult))
            dve.wait_ge(step.sem, step.n)
            for t in range(3):
                V.tensor_reduce(comb[:, t, :], weighted[:, t].rearrange("p k e -> p e k"), AXX,
                                ALU.add).then_inc(S.weights_ready, 1)
            dve.wait_ge(S.weights_ready, 3)

        def largest_counts():
            cnt = s_(c_cnt, 17, slice(0, 1))
            link(V.tensor_reduce(cnt[:, 0:16], bank[3][0:1, 3 * E:4 * E].rearrange("p (a b) -> p a b", b=2), AXX, ALU.max))
            link(V.tensor_reduce(cnt[:, 16:17], cnt[:, 0:16], AXX, ALU.max))
            V.tensor_copy(counts[0:1, 0:17], cnt).then_inc(S.route_ready, 1)

        dve.wait_ge(S.ln1_in, 32)
        attended(0)
        dve.wait_ge(S.router_in, 32)
        link(V.memset(lg[:, 2, :], 0.0))
        attended(1)
        choose(0)
        attended(2)
        choose(1)
        choose(2)
        slot_numbers()

        iota = keep[:, C_IOTA:C_SEL]
        per_slot = [128, 3, 2, SLOTS]
        pick4, pickw4 = (a[:, :, :].rearrange("p t (e s) -> p t e s", e=2) for a in (pick, pickw))

        def pick_slots(i, p, c):
            dve.wait_ge(S.gathered, i * 2)
            dve.wait_ge(S.picked, i * 2)
            slots = iota[:, bass.ds(c * SLOTS, SLOTS)] if not isinstance(c, int) else iota[:, c * SLOTS:(c + 1) * SLOTS]
            V.tensor_tensor(pick4, slots.unsqueeze(1).unsqueeze(1).broadcast_to(per_slot),
                            posm[:, :, pair_of(p)].unsqueeze(3).broadcast_to(per_slot), ALU.is_equal).then_inc(S.picked, 1)

        def weigh_slots(i, p):
            dve.wait_ge(S.pickw_turned, i)
            dve.wait_ge(S.picked, i * 2 + 1)
            V.tensor_tensor(pickw4, pick4, comb[:, :, pair_of(p)].unsqueeze(3).broadcast_to(per_slot),
                            ALU.mult).then_inc(S.picked, 1)

        def swiglu(i):
            dve.wait_ge(S.act_turned, i * 2)
            for n in range(5):
                if n < 4:
                    c = slice(256 * n, 256 * n + 256)
                    dve.wait_ge(S.gate_up_done, i * 4 + (n + 1))
                    V.tensor_scalar(gate[:, c], bank[n][:, 0:512:2], LIMIT, None, ALU.min).then_inc(S.clipped, 1)
                    V.tensor_scalar(up[:, c], bank[n][:, 1:512:2], LIMIT, -LIMIT, ALU.min, ALU.max).then_inc(S.dve_moe, 1)
                    dve.wait_ge(S.clipped, i * 4 + (n + 1))
                    dve.wait_ge(S.dve_moe, i * 8 + (2 * n + 1))
                    V.scalar_tensor_tensor(up[:, c], up[:, c], 1.0, gate[:, c], ALU.add, ALU.mult).then_inc(S.dve_moe, 1)
                if n >= 1:
                    c = slice(256 * n - 256, 256 * n)
                    dve.wait_ge(S.sigmoided, i * 4 + n)
                    dve.wait_ge(S.dve_moe, i * 8 + 2 * n)
                    V.tensor_tensor(up[:, c], up[:, c], sig[:, c], ALU.mult).then_inc(S.act_ready, 1)

        def add_mixed(i):
            for j in range(6):
                t, half = divmod(j, 2)
                n = TILES[t][1]
                c = slice(512 * half, 512 * half + 512)
                dve.wait_ge(S.mixed, i * 6 + (j + 1))
                dve.wait_ge(S.added, i * 6 + (j + 1))
                V.tensor_tensor(acc[0:n, t, c], acc[0:n, t, c], bank[4 + half][0:n, :], ALU.add).then_inc(S.added, 1)

        def start_sums():
            for j in range(6):
                t, half = divmod(j, 2)
                n = TILES[t][1]
                c = slice(512 * half, 512 * half + 512)
                dve.wait_ge(S.spread_down, j + 1)
                V.scalar_tensor_tensor(acc[0:n, t, c], hx[0:n, t, c], ALPHA, bank[4 + half][0:n, :],
                                       ALU.mult, ALU.add).then_inc(S.added, 1)

        dve.wait_ge(S.kstage_stored, stored_after(6))
        pick_slots(0, 0, 0)
        largest_counts()
        weights()
        weigh_slots(0, 0)
        pick_slots(1, 1, 0)
        start_sums()
        swiglu(0)
        with dve.Fori(0, PAIRS - 2) as i:
            weigh_slots(i + 1, i + 1)
            add_mixed(i)
            pick_slots(i + 2, i + 2, 0)
            swiglu(i + 1)
        weigh_slots(PAIRS - 1, PAIRS - 1)
        add_mixed(PAIRS - 2)
        swiglu(PAIRS - 1)
        add_mixed(PAIRS - 1)

        def more(i, p, c, m, odd):
            pick_slots(i, p, c)
            weigh_slots(i, p)
            swiglu(i)
            add_mixed(i)
            dve.wait_ge(S.added, i * 6 + 12)
            dve.sem_inc(S.pass_added, 1)

        def none(i, m, odd):
            for sem, n in ((S.picked, 2), (S.clipped, 4), (S.dve_moe, 8), (S.act_ready, 4), (S.added, 6)):
                skip(dve, sem, i, n, 6 if sem is S.added else 0)

        dve.wait_ge(S.added, 6 * PAIRS + 6)
        further_passes(dve, more, none)
        dve.wait_ge(S.ln2_in, 32)

        def y_statistics(t):
            n = TILES[t][1]
            for half in range(2):
                step.on(V.bn_stats(s_(c_stat + 12 * t + 6 * half, 6, slice(0, n)), acc[0:n, t, 512 * half:512 * half + 512]))
            dve.wait_ge(step.sem, step.n)

        def y_variance(nth):
            y_statistics(ORDER[nth])
            variance(ORDER[nth], S.y_varied)

        def y_scales(nth):
            scales(ORDER[nth], nth, S.y_rooted, S.y_scaled)

        def y_gain(nth):
            gain(acc, ORDER[nth], nth, S.y_centred, S.y_gained)

        y_variance(0)
        y_variance(1)
        y_scales(0)
        y_variance(2)
        y_scales(1)
        y_gain(0)
        y_scales(2)
        y_gain(1)
        y_gain(2)

    ctx.close()


_INS = ["x_prompt", "x_sample", "cache_k_moba", "cache_v_moba", "state_k_win", "state_v_win", "page_table",
        "w_in", "gn_moba", "gn_win", "w_out", "ln1_g", "ln1_b", "w_router", "b_router",
        "w_gate_up", "b_gate_up", "w_down", "b_down", "ln2_g", "ln2_b"]
_OUTS = [(1, SEQ, D), (DB, DS, D), (1, 1, SEQ, H, HD), (1, 1, SEQ, H, HD), (1, DB, DS, H, HD), (1, DB, DS, H, HD),
         (1, 1, SEQ, H, HD), (1, 1, SEQ, H, HD), (1, DB, PAST + DS, H, HD), (1, DB, PAST + DS, H, HD)]


def kernel(**inputs):
    import concourse.bacc as bacc
    from concourse.bass_utils import run_bass_kernel_spmd

    nc = bacc.Bacc("TRN2", target_bir_lowering=False, num_devices=1)
    arrays, args = {}, []
    keep_table, att_table = constant_tables()
    given = {name: inputs[name] for name in _INS} | {"keep_table": keep_table, "att_table": att_table}
    for name, a in given.items():
        a = np.ascontiguousarray(a)
        arrays[f"in_{name}"] = a
        args.append(nc.dram_tensor(f"in_{name}", a.shape, mybir.dt.from_np(a.dtype), kind="ExternalInput").ap())
    for i, shape in enumerate(_OUTS):
        args.append(nc.dram_tensor(f"out_{i}", shape, F32, kind="ExternalOutput").ap())
    build_layer(nc, *args)
    r = run_bass_kernel_spmd(nc, [arrays], core_ids=[0])
    return tuple(r.results[0][f"out_{i}"] for i in range(len(_OUTS)))
```
